# Optimizing a Trainium2 kernel written in Bass

```python
import math
import jax, jax.numpy as jnp
from jax import lax
import numpy as np

D_MODEL = 2048
BATCH = 1
SEQ = 256
DEPTH = 1

ATT_WIDTH = D_MODEL // 2
V_HEAD_DIM = 128
N_ATT_HEADS = ATT_WIDTH // V_HEAD_DIM
QK_HEAD_DIM = V_HEAD_DIM // 2
Q_WIDTH = 2 * N_ATT_HEADS * QK_HEAD_DIM
K_WIDTH = Q_WIDTH
LAMBDA_INIT_BASE = 0.8
LAMBDA_INIT_AMP = 0.6
LAMBDA_INIT_RATE = 0.3
POOL_WIDTH = D_MODEL // 2
POOL_WINDOWS = (2, 4, 8, 16)
POOL_GROUPS = len(POOL_WINDOWS)
POOL_GROUP_WIDTH = POOL_WIDTH // POOL_GROUPS
IN_WIDTH = Q_WIDTH + K_WIDTH + ATT_WIDTH + POOL_WIDTH + 2 * D_MODEL
D_FF = 4 * D_MODEL
PLE_DIM = 256
Q_BLOCK = 128
NORM_EPS = 1e-6

kernel_name = "hybrid_diffattn_pool_gated_block"

def rms_norm(x, g):
    xf = x.astype(jnp.float32)
    y = xf * lax.rsqrt(jnp.mean(xf * xf, axis=-1, keepdims=True) + NORM_EPS)
    return (y * g.astype(jnp.float32)).astype(x.dtype)

def alibi_slopes(n_heads):
    return jnp.asarray(2.0 ** (-8.0 * np.arange(1, n_heads + 1) / n_heads), dtype=jnp.float32)

def diff_attention(q1, q2, k1, k2, v, lam):
    B, H, S, _ = k1.shape
    nb = S // Q_BLOCK
    scale = QK_HEAD_DIM ** -0.5
    slopes = alibi_slopes(H)
    key_pos = jnp.arange(S)

    def to_blocks(q):
        return (q * scale).reshape(B, H, nb, Q_BLOCK, -1).transpose(2, 0, 1, 3, 4)

    def one_block(args):
        qb1, qb2, start = args
        q_pos = start + jnp.arange(Q_BLOCK)
        dist = q_pos[:, None] - key_pos[None, :]
        bias = -slopes[:, None, None] * dist.astype(jnp.float32)
        causal = dist >= 0

        def probs(qb, k):
            s = jnp.einsum('bhqd,bhkd->bhqk', qb, k).astype(jnp.float32) + bias
            s = jnp.where(causal, s, -jnp.inf)
            return jax.nn.softmax(s, axis=-1)

        a = probs(qb1, k1) - lam * probs(qb2, k2)
        return jnp.einsum('bhqk,bhkv->bhqv', a.astype(v.dtype), v)

    starts = jnp.arange(nb) * Q_BLOCK
    out = lax.map(one_block, (to_blocks(q1), to_blocks(q2), starts))
    return out.transpose(1, 2, 0, 3, 4).reshape(B, H, S, V_HEAD_DIM)

def multiscale_pool(u):
    B, S, C = u.shape
    uf = u.astype(jnp.float32)
    csum = jnp.cumsum(uf, axis=1)
    t = jnp.arange(S)
    outs = []
    for g, w in enumerate(POOL_WINDOWS):
        sl = slice(g * POOL_GROUP_WIDTH, (g + 1) * POOL_GROUP_WIDTH)
        cg = csum[..., sl]
        lagged = jnp.pad(cg, ((0, 0), (w, 0), (0, 0)))[:, :S]
        count = jnp.minimum(t + 1, w).astype(jnp.float32)[None, :, None]
        outs.append((cg - lagged) / count - uf[..., sl])
    return jnp.stack(outs, axis=2).astype(u.dtype)

def setup_inputs(seed: int = 0) -> dict:
    key = jax.random.key(seed)
    ks = jax.random.split(key, 24)
    f32 = jnp.float32

    def w(k, shape, fan_in):
        return jax.random.normal(k, shape, f32) * (fan_in ** -0.5)

    def gain(k, shape):
        return 1.0 + 0.02 * jax.random.normal(k, shape, f32)

    return {
        "x": jax.random.normal(ks[0], (BATCH, SEQ, D_MODEL), f32),
        "p": jax.random.normal(ks[1], (DEPTH, BATCH, SEQ, PLE_DIM), f32),
        "norm_mix_g": gain(ks[2], (DEPTH, D_MODEL)),
        "w_in": w(ks[3], (DEPTH, D_MODEL, IN_WIDTH), D_MODEL),
        "lambda_q1": 0.1 * jax.random.normal(ks[4], (DEPTH, QK_HEAD_DIM), f32),
        "lambda_k1": 0.1 * jax.random.normal(ks[5], (DEPTH, QK_HEAD_DIM), f32),
        "lambda_q2": 0.1 * jax.random.normal(ks[6], (DEPTH, QK_HEAD_DIM), f32),
        "lambda_k2": 0.1 * jax.random.normal(ks[7], (DEPTH, QK_HEAD_DIM), f32),
        "subln_g": gain(ks[8], (DEPTH, V_HEAD_DIM)),
        "pool_grp_w": w(ks[9], (DEPTH, POOL_GROUPS, POOL_GROUP_WIDTH, POOL_GROUP_WIDTH), POOL_GROUP_WIDTH),
        "pool_scale": gain(ks[10], (DEPTH, POOL_WIDTH)),
        "w_attn_br": w(ks[11], (DEPTH, ATT_WIDTH, D_MODEL), ATT_WIDTH),
        "w_pool_br": w(ks[12], (DEPTH, POOL_WIDTH, D_MODEL), POOL_WIDTH),
        "w_out": w(ks[13], (DEPTH, D_MODEL, D_MODEL), D_MODEL),
        "norm_mlp_g": gain(ks[14], (DEPTH, D_MODEL)),
        "w_mlp_up": w(ks[15], (DEPTH, D_MODEL, D_FF), D_MODEL),
        "w_mlp_down": w(ks[16], (DEPTH, D_FF, D_MODEL), D_FF),
        "norm_ple_g": gain(ks[17], (DEPTH, D_MODEL)),
        "w_ple": w(ks[18], (DEPTH, PLE_DIM, D_MODEL), PLE_DIM),
        "w_ple_gate": w(ks[19], (DEPTH, D_MODEL, D_MODEL), D_MODEL),
        "final_norm_g": gain(ks[20], (D_MODEL,)),
    }

def reference(x, p, norm_mix_g, w_in, lambda_q1, lambda_k1, lambda_q2, lambda_k2, subln_g,
              pool_grp_w, pool_scale, w_attn_br, w_pool_br, w_out, norm_mlp_g, w_mlp_up,
              w_mlp_down, norm_ple_g, w_ple, w_ple_gate, final_norm_g):
    B, S, _ = x.shape
    H, dqk = N_ATT_HEADS, QK_HEAD_DIM
    o_q = 0
    o_k = o_q + Q_WIDTH
    o_v = o_k + K_WIDTH
    o_u = o_v + ATT_WIDTH
    o_ga = o_u + POOL_WIDTH
    o_gp = o_ga + D_MODEL
    for i in range(DEPTH):
        h = rms_norm(x, norm_mix_g[i])
        z = h @ w_in[i]
        q = z[..., o_q:o_k].reshape(B, S, 2, H, dqk).transpose(2, 0, 3, 1, 4)
        k = z[..., o_k:o_v].reshape(B, S, 2, H, dqk).transpose(2, 0, 3, 1, 4)
        v = z[..., o_v:o_u].reshape(B, S, H, V_HEAD_DIM).transpose(0, 2, 1, 3)
        u = z[..., o_u:o_ga]
        gate_a = jax.nn.sigmoid(z[..., o_ga:o_gp])
        gate_p = jax.nn.sigmoid(z[..., o_gp:])

        lam_init = LAMBDA_INIT_BASE - LAMBDA_INIT_AMP * math.exp(-LAMBDA_INIT_RATE * i)
        lam = (jnp.exp(jnp.sum(lambda_q1[i].astype(jnp.float32) * lambda_k1[i].astype(jnp.float32)))
               - jnp.exp(jnp.sum(lambda_q2[i].astype(jnp.float32) * lambda_k2[i].astype(jnp.float32)))
               + lam_init)
        o = diff_attention(q[0], q[1], k[0], k[1], v, lam)
        o = rms_norm(o, subln_g[i]) * (1.0 - lam_init)
        o = o.transpose(0, 2, 1, 3).reshape(B, S, ATT_WIDTH)
        a_branch = o @ w_attn_br[i]

        pooled = multiscale_pool(u)
        pm = jnp.einsum('bsgc,gcd->bsgd', pooled, pool_grp_w[i]).reshape(B, S, POOL_WIDTH)
        p_branch = (pm * pool_scale[i]) @ w_pool_br[i]

        merged = gate_a * a_branch + gate_p * p_branch
        x = x + merged @ w_out[i]

        hm = rms_norm(x, norm_mlp_g[i])
        x = x + jnp.square(jax.nn.relu(hm @ w_mlp_up[i])) @ w_mlp_down[i]

        ple_gate = jax.nn.sigmoid(rms_norm(x, norm_ple_g[i]) @ w_ple_gate[i])
        x = x + (p[i] @ w_ple[i]) * ple_gate
    return rms_norm(x, final_norm_g)


_drawn_inputs = setup_inputs


def setup_inputs(seed=0):
    import zlib

    import numpy as np

    out = dict(_drawn_inputs(seed))
    spreads = {}
    factors = {'norm_mix_g': 3.467,
     'lambda_k1': 4.625,
     'lambda_q2': 12.973,
     'subln_g': 200.0,
     'pool_scale': 63.02,
     'norm_mlp_g': 11.529,
     'norm_ple_g': 200.0,
     'final_norm_g': 24.051,
     'p': 8.0,
     'w_ple': 8.0,
     'w_ple_gate': 8.0}
    for name, (base, spread) in spreads.items():
        noise = np.random.default_rng([zlib.crc32(name.encode()), seed]).standard_normal(out[name].shape)
        drawn = base * np.exp(spread * noise) if base else spread * noise
        out[name] = __import__('jax').numpy.asarray(drawn.astype(out[name].dtype))
    for name, factor in factors.items():
        out[name] = (out[name] * factor).astype(out[name].dtype)
    return out
```

```python
from contextlib import ExitStack

import concourse.bass as bass
from concourse import mybir

F32 = mybir.dt.float32
F32R = mybir.dt.float32r
ACT = mybir.ActivationFunctionType
ALU = mybir.AluOpType
AX = mybir.AxisListType

P = 128
SEQ = 256
D = 2048
D_FF = 4 * D
HEADS = 8
DV = 128
DQK = 64
WINDOWS = (2, 4, 8, 16)
EPS = 1e-6
LAM_INIT = 0.8 - 0.6
NEG = -3.0e38

DB = D // P
GB = 4
GW = GB * P
UNIT = 2 * GW
RING = 4
LEAD = 5
CHUNK = D // GW
TRI = 3 * P

COLS = {}
_at = 0
for _name, _n in (("norm_mix", DB), ("norm_mlp", DB), ("norm_ple", DB), ("norm_final", DB), ("pool_scale", 8),
                  ("subln", 1), ("score_scale", HEADS), ("slope", HEADS), ("inv_count", 64)):
    COLS[_name] = (_at, _n)
    _at += _n
N_COLS = _at


PAIRED = ("slot", "mix", "wple", "ple")
TWO_BANKS = PAIRED + ("v",)


class Phase:

    def __init__(self, kind, upg, groups, unit0, group0, index0, quarter, low0, drained0):
        self.kind, self.upg, self.groups, self.quarter = kind, upg, groups, quarter
        self.unit0, self.group0, self.index0, self.low0, self.drained0 = unit0, group0, index0, low0, drained0


def plan():
    phases, unit, group, low, drained, seen = {}, 0, 0, 0, 0, {}
    for name, kind, upg, groups, quarter in (
            ("qk", "qk", 8, 4, 0), ("v", "v", 8, 2, 0), ("slot", "slot", 8, 10, 0), ("ab0", "ab", 4, 2, 0),
            ("mix", "mix", 1, 2, 0), ("ab1", "ab", 4, 2, 0), ("pb", "pb", 4, 4, 0),
            ("wout", "wout", 8, 4, 0), ("up0", "up", 8, 4, 0), ("down0", "down", 8, 4, 0),
            ("wple", "wple", 1, 4, 0), ("up1", "up", 8, 4, 1), ("down1", "down", 8, 4, 1),
            ("again", None, 8, 8, 2),
            ("up3", "up", 8, 4, 3), ("downl", "downl", 8, 4, 3), ("ple", "ple", 8, 4, 0)):
        phases[name] = Phase(kind, upg, groups, unit, group, seen.get(kind, 0), quarter, low, drained)
        unit += upg * groups
        group += groups
        low += 0 if kind in TWO_BANKS else groups
        drained += 0 if kind in ("v", "slot", "wple") else groups
        for k in ((kind,) if kind else ("up", "down")):
            seen[k] = seen.get(k, 0) + (groups if kind else groups // 2)
    return phases, unit


PH, UNITS = plan()
LAST_GROUP = PH["ple"].group0 + PH["ple"].groups - 1
SQUARES_AT = (3, 4, 6, 7)
FINAL_PIECES = ((0, 1), (1, 2), (3, 2), (5, 2), (7, 2), (9, 3))
REPEAT = 8


def walk(eng, pair):

    def run(name, first, last, r=0):
        with eng.Fori(first, last) as i:
            pair(PH[name], i, r)

    pair(PH["qk"], 0, 0)
    pair(PH["qk"], 1, 0)
    pair(PH["v"], 0, 0)
    run("slot", 0, 4)
    pair(PH["slot"], 4, 0)
    pair(PH["ab0"], 0, 0)
    pair(PH["mix"], 0, 0)
    pair(PH["ab1"], 0, 0)
    run("pb", 0, 2)
    run("wout", 0, 2)
    pair(PH["up0"], 0, 0)
    pair(PH["up0"], 1, 0)
    run("down0", 0, 2)
    pair(PH["wple"], 0, 0)
    pair(PH["wple"], 1, 0)
    with eng.Fori(0, 2) as r:
        run("up1", 0, 2, r)
        run("down1", 0, 2, r)
    run("up3", 0, 2)
    run("downl", 0, 2)
    pair(PH["ple"], 0, 0)
    pair(PH["ple"], 1, 0)


def unit_index(ph, i, r, u):
    return i * (2 * ph.upg) + r * (REPEAT * 8) + (ph.unit0 + u)


def group_index(ph, i, r, half):
    return i * 2 + r * REPEAT + (ph.group0 + half)


def units_summed(ph, i, r, half):
    return unit_index(ph, i, r, (half + 1) * ph.upg)


def kind_index(ph, i, r, half):
    return i * 2 + r * (REPEAT // 2) + (ph.index0 + half)


def slot_of(ph, i, u):
    return (ph.unit0 + u + (2 * ph.upg * i if isinstance(i, int) else 0)) % RING


def loads_of_slot(ph, i, r, u):
    if isinstance(i, int):
        return (ph.unit0 + 2 * ph.upg * i + u) // RING + 1
    return i * (2 * ph.upg // RING) + r * (REPEAT * 8 // RING) + ((ph.unit0 + u) // RING + 1)


def low_count(ph, i, r, half):
    return i * 2 + r * REPEAT + (ph.low0 + half)


def drained_count(ph, i, r, half):
    return i * 2 + r * REPEAT + (ph.drained0 + half)


def drains_at(ph, j):
    if ph.upg == 1:
        return [(j, 0)]
    half, step = divmod(j, ph.upg)
    step -= ph.upg - 3
    return [(half, step)] if step >= 0 else []


def banks(ph, half, i=0):
    if ph.kind == "slot":
        return 2 * half
    if ph.kind == "mix":
        return 4 + 2 * half
    if ph.kind == "wple":
        return 4 * i + 2 * half
    return 4 * (1 - half) if ph is PH["ab0"] else 4 * half


def freed_before(ph, i, r, half):
    g = group_index(ph, i, r, half)
    if isinstance(g, int) and g < 2:
        return 0
    if ph.kind == "mix":
        return g - (1 + half)
    if ph is PH["ab1"] and half == 0:
        return g - 2
    if ph.kind == "wple":
        return ph.group0 - 1 + i
    return g - 1


def build(nc, d, out):
    with ExitStack() as ctx:
        def sb(name, shape, dt=F32):
            return ctx.enter_context(nc.sbuf_tensor(name, shape, dt))

        def sem(name):
            return ctx.enter_context(nc.semaphore(name))

        stage = sb("stage", [P, RING, UNIT])
        w_hi = sb("w_hi", [P, RING, UNIT], F32R)
        w_lo = sb("w_lo", [P, RING, UNIT], F32R)
        opA = sb("opA", [P, DB, 2 * SEQ], F32R)
        opB = sb("opB", [P, DB, 2 * SEQ], F32R)
        ug_offset = nc.sbuf_base
        ug = sb("ug", [P, 40, SEQ])
        p_parts = nc.alloc_sbuf_tensor_at("p_parts", [P, 2, 2 * SEQ], F32R, offset=ug_offset)
        gate_a, gate_p = ug[:, 8:24, :], ug[:, 24:40, :]
        xv = sb("xv", [P, 24, SEQ])
        res = xv[:, 0:DB, :]
        t = sb("t", [P, GB, SEQ])
        y = sb("y", [P, GB, SEQ])
        z = sb("z", [P, GB, SEQ])
        pr = sb("pr", [P, 2, TRI])
        aT = sb("aT", [P, TRI])
        neg_dist = sb("neg_dist", [P, TRI])
        qk = sb("qk", [P, 4, SEQ])
        v_pair = sb("v_pair", [P, 2, SEQ])
        ssq = qk
        sq_sum = sb("sq_sum", [P, SEQ])
        rstd = sb("rstd", [P, SEQ])
        diag = sb("diag", [P, SEQ])
        ident = sb("ident", [P, P])
        ones = sb("ones", [P, P])
        cols = sb("cols", [P, N_COLS])
        small = sb("small", [P, 104])
        lam_in = small[0:DQK, 0:4]
        lam_prod = small[0:DQK, 4:6]
        lam_exp = small[:, 6:8]
        neg_lam = small[:, 8:9]
        subln = small[:, 9:10]
        row_max = small[:, 12:16]
        exp_bias = small[:, 16:20]
        sums = small[:, 20:24]
        recip = small[:, 24:28]
        recip_lam = small[:, 28:30]
        o_ssq = small[:, 32:48]
        o_ms = small[:, 48:64]
        o_root = small[:, 64:80]
        o_corr = small[:, 80:96]
        ms, root, corr, rstd_col = small[:, 96:98], small[:, 98:100], small[:, 100:102], small[:, 102:104]
        p_in = ug[:, 4:6, :]

        ps = ctx.enter_context(nc.psum_tensor("ps", [P, 8, 512], F32))

        def col(name, a=0, n=1):
            return cols[:, bass.ds(a + COLS[name][0], n)]

        def gains(name, a, n=GB):
            return col(name, a, n).unsqueeze(2).to_broadcast([P, n, SEQ])

        def all_blocks(row):
            return row.unsqueeze(1).to_broadcast([P, GB, SEQ])

        loaded = [sem(f"loaded{s}") for s in range(RING)]
        hi_ready, lo_ready, unit_done = sem("hi_ready"), sem("lo_ready"), sem("unit_done")
        first_loaded, first_hi, first_lo = sem("first_loaded"), sem("first_hi"), sem("first_lo")
        psum_free, drained = sem("psum_free"), sem("drained")
        low_copied = sem("low_copied")
        x_loaded = [sem(f"x_loaded{e}") for e in range(8)]
        x_again = [sem(f"x_again{q}") for q in range(4)]
        cols_loaded, lam_loaded, p_loaded = sem("cols_loaded"), sem("lam_loaded"), sem("p_loaded")
        consts_started, consts_ready = sem("consts_started"), sem("consts_ready")
        lam_step, lam_summed, lam_exped = sem("lam_step"), sem("lam_summed"), sem("lam_exped")
        subln_ready, neg_lam_ready = sem("subln_ready"), sem("neg_lam_ready")
        xg_scaled, xg_hi, xg_ready = sem("xg_scaled"), sem("xg_hi"), sem("xg_ready")
        squared, ssq_part, ssq_joined = sem("squared"), sem("ssq_part"), sem("ssq_joined")
        ssq_summed, ms_ready = sem("ssq_summed"), sem("ms_ready")
        recip_ready, root_ready = sem("recip_ready"), sem("root_ready")
        newton, rstd_ready = sem("newton"), sem("rstd_ready")
        diag_ready, rstd_spread = sem("diag_ready"), sem("rstd_spread")
        front_summed, tail_scaled, tail_gate, tail_step, tail_squared = (
            sem("front_summed"), sem("tail_scaled"), sem("tail_gate"), sem("tail_step"), sem("tail_squared"))
        pair_copied, scores_ready, scores_biased = sem("pair_copied"), sem("scores_ready"), sem("scores_biased")
        max_ready, bias_ready, probs_ready = sem("max_ready"), sem("bias_ready"), sem("probs_ready")
        recip_sums, first_scaled, attn_ready = sem("recip_sums"), sem("first_scaled"), sem("attn_ready")
        attn_turned, turned_copied = sem("attn_turned"), sem("turned_copied")
        pv_ready, head_done = sem("pv_ready"), sem("head_done")
        o_ms_ready, o_recip, o_rooted, o_newton = sem("o_ms_ready"), sem("o_recip"), sem("o_rooted"), sem("o_newton")
        o_scaled, o_turned, o_copied = sem("o_scaled"), sem("o_turned"), sem("o_copied")
        o_hi, o_ready = sem("o_hi"), sem("o_ready")
        pool_step, pooled = sem("pool_step"), sem("pooled")
        pooled_hi, pooled_ready = sem("pooled_hi"), sem("pooled_ready")
        p_hi, p_ready = sem("p_hi"), sem("p_ready")
        sigmoid_ready = {k: sem(f"sigmoid_ready_{k}") for k in ("ab", "pb", "ple")}
        stepped = {k: sem(f"stepped_{k}") for k in ("pb", "wout", "downl", "ple")}
        z_ready = {k: sem(f"z_ready_{k}") for k in ("mix", "pb", "wout", "up", "downl")}
        z_hi = {k: sem(f"z_hi_{k}") for k in ("mix", "pb", "wout", "up", "downl")}
        gated, three_joined = sem("gated"), sem("three_joined")
        final_scaled, stored = sem("final_scaled"), sem("stored")

        operand = {"qk": opA, "v": opA, "slot": opA, "ab": opB[:, 0:8, :], "mix": opB[:, 8:16, :], "pb": opA,
                   "wout": opB, "wple": p_parts, "up": opA, "down": opB, "downl": opB, "ple": opA}
        made_by = {"pb": "mix", "wout": "pb", "up0": "wout", "up1": "wout", "up3": "wout", "down0": "up0",
                   "down1": "up1", "downl": "up3", "ple": "downl"}
        made_by = {PH[name]: PH[maker] for name, maker in made_by.items()}
        norm_of = {"qk": 0, "up": 1, "ple": 2}

        def norm_bank(k):
            return (0, 7, 7, 7)[k]

        def has_norm(ph, i):
            return ph in (PH["qk"], PH["up0"], PH["ple"]) and isinstance(i, int) and i == 0

        block = ctx.enter_context(nc.Block())

        def load_x_by(eng, b0, n, signal):
            eng.dma_start(res[:, b0:b0 + n, :],
                          d["x"][b0 * P:(b0 + n) * P, :].rearrange("(b p) t -> p b t", p=P)).then_inc(signal, 16)

        @block.sync
        def _(sp):
            def weights(ph, i, r, u):
                half, k = divmod(u, ph.upg)
                if ph.kind == "mix":
                    return d["pool_grp_w"][u * 512:(u + 1) * 512, :].rearrange("(b p) n -> p b n", p=P)
                name = {"qk": "w_in", "v": "w_in", "slot": "w_in", "ab": "w_attn_br", "pb": "w_pool_br", "wout": "w_out",
                        "wple": "w_ple", "up": "w_mlp_up", "down": "w_mlp_down", "downl": "w_mlp_down",
                        "ple": "w_ple_gate"}[ph.kind]
                skip = {"ab": ph.index0, "v": PH["v"].group0, "slot": PH["slot"].group0}.get(ph.kind, 0)
                group = i * 2 + (half + skip)
                row = 2 * P * k
                if ph.kind == "up":
                    group = i * 2 + (r + ph.quarter) * CHUNK + half
                if ph.kind in ("down", "downl"):
                    row = (r + ph.quarter) * D + row
                return d[name][bass.ds(row, 2 * P), bass.ds(group * GW, GW)].rearrange("(b p) n -> p b n", p=P)

            def load(ph, i, r, u):
                n = unit_index(ph, i, r, u)
                if isinstance(n, int) and n == 0:
                    for kk, signal in ((0, first_loaded), (1, loaded[0])):
                        sp.dma_start(stage[:, 0, kk * GW:(kk + 1) * GW],
                                     d["w_in"][kk * P:(kk + 1) * P, 0:GW]).then_inc(signal, 16)
                    return
                if not (isinstance(n, int) and n < RING):
                    sp.wait_ge(lo_ready, n - (RING - 1))
                s = slot_of(ph, i, u)
                dst = stage[:, s, :].rearrange("p (b n) -> p b n", b=4 if ph.kind == "mix" else 2)
                sp.dma_start(dst, weights(ph, i, r, u)).then_inc(loaded[s], 16)

            def pair(ph, i, r):
                if ph.kind == "slot" and isinstance(i, int):
                    sp.wait_ge(pair_copied, 2 * 4)
                    for q in range(4):
                        load_x_by(sp, 4 * q, 4, x_again[q])
                if ph.kind == "ab" and ph.index0 == 2:
                    sp.wait_ge(pooled_ready, 2)
                    sp.dma_start(p_in, d["p"].rearrange("(b p) t -> p b t", p=P)).then_inc(p_loaded, 16)
                for u in range(2 * ph.upg):
                    if ph is PH["qk"] and i == 0 and u < 8:
                        load_x_by(sp, 2 * u, 2, x_loaded[u])
                    load(ph, i, r, u)

            walk(sp, pair)

            def store(b0, n, scaled):
                sp.wait_ge(final_scaled, scaled)
                sp.dma_start(out[b0 * P:(b0 + n) * P, :].rearrange("(b p) t -> p b t", p=P),
                             res[:, b0:b0 + n, :]).then_inc(stored, 16)

            for n, (b0, blocks) in enumerate(FINAL_PIECES):
                store(b0, blocks, n + 1)
            for n in range(2):
                store(DB - GB + 2 * n, 2, len(FINAL_PIECES) + 2 * n + 2)
            sp.wait_ge(stored, (len(FINAL_PIECES) + 2) * 16)

        @block.gpsimd
        def _(pool):
            pool.memset(ident[:, :], 0.0).then_inc(consts_started, 1)
            for n, base in ((0, 0), (1, -P), (2, 0)):
                pool.iota(neg_dist[:, n * P:(n + 1) * P], pattern=[[1, P]], base=base, channel_multiplier=-1,
                          allow_small_or_imprecise_dtypes=True).then_inc(consts_started, 1)
            pool.memset(ones[:, :], 1.0).then_inc(consts_ready, 1)
            pool.wait_ge(consts_started, 4)
            pool.affine_select(out=ident[:, :], in_=ident[:, :], compare_op=ALU.not_equal, fill=1.0, base=0,
                               pattern=[[-1, P]], channel_multiplier=1).then_inc(consts_ready, 1)
            for n in (0, 2):
                part = neg_dist[:, n * P:(n + 1) * P]
                pool.affine_select(out=part, in_=part, compare_op=ALU.is_ge, fill=NEG, base=0,
                                   pattern=[[-1, P]], channel_multiplier=1).then_inc(consts_ready, 1)

        @block.tensor
        def _(pe):
            def last_products(ph, i):
                pe.wait_ge(lo_ready, UNITS)
                for bank in range(2):
                    for u in (2 * ph.upg - 2, 2 * ph.upg - 1):
                        s = slot_of(ph, i, u)
                        for kk in range(2):
                            kb = 2 * (u - ph.upg) + kk
                            x, last = opA[:, kb, :], kb == DB - 1
                            for b in (2 * bank, 2 * bank + 1):
                                at = kk * GW + b * P
                                hi, lo = w_hi[:, s, at:at + P], w_lo[:, s, at:at + P]
                                o = ps[:, banks(ph, 1) + bank, (b % 2) * SEQ:(b % 2 + 1) * SEQ]
                                pe.matmul(o, hi, x[:, 0:SEQ], start=False, stop=False, skip_group_check=True)
                                pe.matmul(o, hi, x[:, SEQ:], start=False, stop=False, skip_group_check=True)
                                mm = pe.matmul(o, lo, x[:, 0:SEQ], start=False, stop=last, skip_group_check=True)
                    mm.then_inc(front_summed if bank == 0 else unit_done, 1)

            def unit_products(ph, i, r, u):
                half, k = divmod(u, ph.upg)
                n = unit_index(ph, i, r, u)
                s = slot_of(ph, i, u)
                op = operand[ph.kind]
                bank = banks(ph, half, i)
                if isinstance(n, int) and n == 0:
                    pe.wait_ge(first_lo, 1)
                else:
                    pe.wait_ge(lo_ready, n + 1)
                for kk in range(2):
                    if kk == 1 and isinstance(n, int) and n == 0:
                        pe.wait_ge(lo_ready, 1)
                    kb = 2 * k + kk
                    first, last = kb == 0, kb == 2 * ph.upg - 1
                    for b in range(GB):
                        if ph.kind == "mix":
                            g, nb = divmod(b, 2)
                            at = (2 * g + kk) * 256 + nb * P
                            x = op[:, (2 * u + g) * 2 + kk, :]
                            first, last = kk == 0, kk == 1
                        else:
                            at = kk * GW + b * P
                            x = op[:, kb, :]
                        hi, lo = w_hi[:, s, at:at + P], w_lo[:, s, at:at + P]
                        if ph.kind in PAIRED:
                            o = ps[:, bank + b // 2, (b % 2) * SEQ:(b % 2 + 1) * SEQ]
                            pe.matmul(o, hi, x[:, 0:SEQ], start=first and b % 2 == 0, stop=False, skip_group_check=True)
                            pe.matmul(o, hi, x[:, SEQ:], start=False, stop=False, skip_group_check=True)
                            mm = pe.matmul(o, lo, x[:, 0:SEQ], start=False, stop=last, skip_group_check=True)
                        else:
                            pe.matmul(ps[:, bank + b, :], hi, x, start=first, stop=False, skip_group_check=True)
                            mm = pe.matmul(ps[:, bank + b, 0:SEQ], lo, x[:, 0:SEQ], start=False, stop=last,
                                           skip_group_check=True)
                mm.then_inc(unit_done, 1)

            def v_products(ph, i, u):
                half, k = divmod(u, ph.upg)
                s = slot_of(ph, i, u)
                pe.wait_ge(lo_ready, unit_index(ph, i, 0, u) + 1)
                for kk in range(2):
                    kb = 2 * k + kk
                    hi, lo = (w[:, s, kk * GW:(kk + 1) * GW] for w in (w_hi, w_lo))
                    for h in range(2):
                        o = ps[:, banks(ph, half) + h, :]
                        x_hi, x_lo = (opA[:, kb, m * SEQ + h * P:m * SEQ + (h + 1) * P] for m in range(2))
                        pe.matmul(o, x_hi, hi, start=kb == 0, stop=False, skip_group_check=True)
                        pe.matmul(o, x_hi, lo, start=False, stop=False, skip_group_check=True)
                        mm = pe.matmul(o, x_lo, hi, start=False, stop=kb == DB - 1, skip_group_check=True)
                mm.then_inc(unit_done, 1)

            def scores(i, hh):
                if hh == 0:
                    pe.wait_ge(pair_copied, i * 2 + 1)
                pe.wait_ge(scores_biased, i * 2 + (hh + 1))
                part = slice(DQK * hh, DQK * hh + DQK)
                for m in range(2):
                    pe.matmul(ps[:, 4 + m, 0:P], qk[part, m, 0:P], qk[part, 2 + m, 0:P], start=True, stop=True,
                              skip_group_check=True)
                    mm = pe.matmul(ps[:, 4 + m, P:TRI], qk[part, m, P:2 * P], qk[part, 2 + m, :], start=True, stop=True,
                                   skip_group_check=True)
                mm.then_inc(scores_ready, 1)

            def turn(i, hh):
                pe.wait_ge(attn_ready, i * 4 + 2 * hh + 2)
                pe.wait_ge(head_done, i * 6 + (3 * hh + 1))
                for b in range(3):
                    mm = pe.transpose(ps[:, 6, b * P:(b + 1) * P], pr[:, 0, b * P:(b + 1) * P], ident[:, :])
                mm.then_inc(attn_turned, 1)

            def attn_v(i, hh):
                pe.wait_ge(turned_copied, i * 2 + (hh + 1))
                pe.wait_ge(pair_copied, i * 2 + 2)
                pe.matmul(ps[:, 7, 0:P], aT[:, 0:P], v_pair[:, hh, 0:P], start=True, stop=True, skip_group_check=True)
                pe.matmul(ps[:, 7, P:2 * P], aT[:, P:2 * P], v_pair[:, hh, 0:P], start=True, stop=False,
                          skip_group_check=True)
                pe.matmul(ps[:, 7, P:2 * P], aT[:, 2 * P:], v_pair[:, hh, P:], start=False, stop=True,
                          skip_group_check=True).then_inc(pv_ready, 1)

            def turn_o():
                pe.wait_ge(o_scaled, 1)
                for h in range(HEADS):
                    for b in range(2):
                        mm = pe.transpose(ps[:, 4 + h // 2, (h % 2) * SEQ + b * P:(h % 2) * SEQ + (b + 1) * P],
                                          xv[:, 16 + h, b * P:(b + 1) * P], ident[:, :])
                mm.then_inc(o_turned, 1)

            def sum_squares(k, bank):
                pe.wait_ge(ssq_joined, k + 1)
                for h in range(2):
                    mm = pe.matmul(ps[:, bank, h:h + 1], sq_sum[:, h * P:(h + 1) * P], ones[:, 0:1], start=h == 0,
                                   stop=True, skip_group_check=True)
                mm.then_inc(ssq_summed, 1)

            def spread(k, bank):
                pe.wait_ge(diag_ready, 2 * k + 2)
                pe.matmul(ps[:, bank, 0:SEQ], ones[:, :], diag[:, :], start=True, stop=True,
                          skip_group_check=True).then_inc(rstd_spread, 1)

            def sum_last_squares(bank):
                pe.wait_ge(three_joined, 1)
                for h in range(2):
                    pe.matmul(ps[:, bank, h:h + 1], sq_sum[:, h * P:(h + 1) * P], ones[:, 0:1], start=h == 0,
                              stop=False, skip_group_check=True)
                for b in range(GB):
                    if b % 2 == 0:
                        pe.wait_ge(tail_squared, b // 2 + 1)
                    for h in range(2):
                        mm = pe.matmul(ps[:, bank, h:h + 1], t[:, b, h * P:(h + 1) * P], ones[:, 0:1], start=False,
                                       stop=b == GB - 1, skip_group_check=True)
                mm.then_inc(ssq_summed, 1)

            def pair(ph, i, r):
                first_pair = ph is PH["qk"] and i == 0
                for u in range(2 * ph.upg):
                    half, k = divmod(u, ph.upg)
                    g = group_index(ph, i, r, half)
                    if k == 0:
                        freed = freed_before(ph, i, r, half)
                        if not (isinstance(freed, int) and freed == 0):
                            pe.wait_ge(psum_free, freed)
                        if half == 1 and ph is PH["up0"] and i == 0:
                            pe.wait_ge(rstd_ready, 2)
                        if isinstance(g, int) and g == PH["ab0"].group0:
                            pe.wait_ge(o_ready, 2)
                    if ph.kind in ("qk", "v"):
                        pe.wait_ge(xg_ready, k + 1)
                    elif ph.kind == "ab":
                        pe.wait_ge(o_ready, k // 2 + 1)
                    elif ph.kind == "mix":
                        pe.wait_ge(pooled_ready, u + 1)
                    elif ph.kind == "wple":
                        pe.wait_ge(p_ready, 1)
                    elif ph in made_by:
                        again = r * REPEAT if ph.kind == "down" else 0
                        pe.wait_ge(drained, again + (made_by[ph].drained0 + k // 2 + 1))
                    if ph is PH["ple"] and i == 1 and u >= 14:
                        if u == 14:
                            last_products(ph, i)
                        continue
                    if ph.kind == "v":
                        v_products(ph, i, u)
                    else:
                        unit_products(ph, i, r, u)
                    if ph.kind == "slot" and not isinstance(i, int):
                        if u == 2:
                            scores(i, 0)
                        if u == 6:
                            turn(i, 0)
                            scores(i, 1)
                        if u == 9:
                            attn_v(i, 0)
                        if u == 11:
                            turn(i, 1)
                        if u == 14:
                            attn_v(i, 1)
                    if ph.kind == "slot" and isinstance(i, int) and u == 5:
                        turn_o()
                    if first_pair:
                        if u == 11:
                            pe.wait_ge(psum_free, 1)
                            pe.wait_ge(lam_step, 1)
                            pe.matmul(ps[:, 2, 0:2], ones[0:DQK, :], lam_prod, start=True,
                                      stop=True).then_inc(lam_summed, 1)
                            sum_squares(0, norm_bank(0))
                        if u == 13:
                            spread(0, norm_bank(0))
                        if u == 15:
                            pe.wait_ge(lam_exped, 1)
                            pe.wait_ge(rstd_ready, 1)
                    elif has_norm(ph, i):
                        if u == 5:
                            pe.wait_ge(psum_free, g)
                            sum_squares(norm_of[ph.kind], norm_bank(norm_of[ph.kind]))
                        if u == 6:
                            spread(norm_of[ph.kind], norm_bank(norm_of[ph.kind]))

            pe.sem_inc(attn_turned, 1)
            pe.wait_ge(consts_ready, 4)
            walk(pe, pair)
            sum_last_squares(norm_bank(3))
            spread(3, norm_bank(3))

        @block.scalar
        def _(act):
            def split_hi(ph, i, r, u):
                n = unit_index(ph, i, r, u)
                if isinstance(n, int) and n >= UNITS:
                    return
                s = slot_of(ph, i, u)
                if isinstance(n, int) and n == 0:
                    act.wait_ge(first_loaded, 16)
                    act.activation(w_hi[:, 0, 0:GW], stage[:, 0, 0:GW], ACT.Copy).then_inc(first_hi, 1)
                    act.wait_ge(loaded[0], 16)
                    act.activation(w_hi[:, 0, GW:], stage[:, 0, GW:], ACT.Copy).then_inc(hi_ready, 1)
                    return
                act.wait_ge(loaded[s], loads_of_slot(ph, i, r, u) * 16)
                if not (isinstance(n, int) and n < RING):
                    act.wait_ge(unit_done, n - (RING - 1))
                act.activation(w_hi[:, s, :], stage[:, s, :], ACT.Copy).then_inc(hi_ready, 1)

            def copy_low(ph, i, r, half):
                bank = banks(ph, half)
                act.wait_ge(unit_done, units_summed(ph, i, r, half))
                before = drained_count(ph, i, r, half)
                if isinstance(before, int) and before == 0:
                    act.wait_ge(ssq_part, 2)
                else:
                    act.wait_ge(drained, before)
                act.activation(t[:, :, :], ps[:, bank:bank + GB, SEQ:], ACT.Copy).then_inc(low_copied, 1)

            def open_gate(ph, i, half):
                kc = kind_index(ph, i, 0, half)
                gate = (gate_a if ph.kind == "ab" else gate_p)[:, bass.ds(kc * GB, GB), :]
                act.activation(gate, gate, ACT.Sigmoid).then_inc(sigmoid_ready[ph.kind], 1)

            def hi_part(kind, dst, src, kc):
                act.wait_ge(z_ready[kind], kc + 1)
                act.activation(dst, src, ACT.Copy).then_inc(z_hi[kind], 1)

            def square_res(b0):
                act.activation(t[:, :, :], res[:, bass.ds(b0, GB), :], ACT.Square).then_inc(squared, 1)

            def drain(ph, i, r, half, step):
                kind, g, kc = ph.kind, group_index(ph, i, r, half), kind_index(ph, i, r, half)
                blocks = bass.ds(kc * GB, GB)
                if kind == "wple":
                    act.wait_ge(psum_free, g)
                    act.wait_ge(unit_done, units_summed(ph, i, r, half))
                    bank = banks(ph, half, i)
                    act.activation(gate_a[:, blocks, :].rearrange("p b t -> p (b t)"),
                                   ps[:, bank:bank + 2, :].rearrange("p b t -> p (b t)"), ACT.Copy).then_inc(psum_free, 1)
                if kind in ("v", "slot", "wple"):
                    return
                if isinstance(g, int) and g == LAST_GROUP:
                    if step == 1:
                        last_drain()
                    return
                if step == 0 and kind not in TWO_BANKS:
                    copy_low(ph, i, r, half)
                if step == 1:
                    if kind in ("wout", "downl"):
                        act.wait_ge(stepped[kind], kc + 1)
                        square_res(kc * GB)
                    if kind == "ple":
                        act.wait_ge(psum_free, g + 1)
                        act.activation(y[:, :, :], z[:, :, :], ACT.Sigmoid).then_inc(sigmoid_ready["ple"], 1)
                if step == 2:
                    if kind == "mix":
                        act.wait_ge(psum_free, g + 1)
                        act.activation(opA[:, blocks, 0:SEQ], (z, y)[half][:, :, :], ACT.Copy).then_inc(z_hi[kind], 1)
                    if kind in ("wout", "downl"):
                        hi_part(kind, opA[:, blocks, 0:SEQ], z[:, :, :], kc)
                    if kind == "pb":
                        hi_part(kind, opB[:, blocks, 0:SEQ], z[:, :, :], kc)
                    if kind == "up":
                        act.wait_ge(z_ready[kind], kc + 1)
                        for into in (opB[:, bass.ds(i * 8 + half * GB, GB), 0:SEQ], y[:, :, :]):
                            act.activation(into, z[:, :, :], ACT.Square).then_inc(z_hi[kind], 1)
                    if kind == "ple":
                        act.wait_ge(stepped[kind], kc + 1)
                        act.wait_ge(drained, drained_count(ph, i, r, half))
                        square_res(kc * GB)

            def xg_part_hi(e):
                act.wait_ge(xg_scaled, e + 1)
                act.activation(opA[:, 2 * e:2 * e + 2, 0:SEQ], z[:, 2 * (e % 2):2 * (e % 2) + 2, :],
                               ACT.Copy).then_inc(xg_hi, 1)

            def exps(i, hh):
                act.wait_ge(bias_ready, i * 2 + (hh + 1))
                slope = col("slope", i * 2 + hh)
                for b, (a, e) in enumerate(((0, P), (P, TRI))):
                    for m in range(2):
                        r = 2 * b + m
                        act.activation(pr[:, m, a:e], pr[:, m, a:e], ACT.Exp, bias=exp_bias[:, r:r + 1], scale=slope,
                                       accum_out=sums[:, r:r + 1]).then_inc(probs_ready, 1)

            def copy_turned(i, hh):
                act.wait_ge(attn_turned, i * 2 + (hh + 2))
                act.activation(aT[:, :], ps[:, 6, 0:TRI], ACT.Copy).then_inc(turned_copied, 1)

            def copy_out(i, hh):
                act.wait_ge(pv_ready, i * 2 + (hh + 1))
                act.activation(xv[:, bass.ds(i * 2 + (16 + hh), 1), :], ps[:, 7:8, 0:SEQ], ACT.Copy).then_inc(head_done, 1)
                for b in range(2):
                    act.activation(aT[:, b * P:(b + 1) * P], ps[:, 7, b * P:(b + 1) * P], ACT.Square,
                                   accum_out=o_ssq[:, bass.ds(i * 4 + (2 * hh + b), 1)]).then_inc(head_done, 1)

            def last_drain():
                for h in range(2):
                    part = slice(2 * h, 2 * h + 2)
                    act.wait_ge(tail_scaled, h + 1)
                    act.activation(y[:, part, :], z[:, part, :], ACT.Sigmoid).then_inc(tail_gate, 1)
                    if h == 0:
                        act.wait_ge(ssq_part, 15)
                    else:
                        act.activation(o_root[:, 0:1], o_ms[:, 0:1], ACT.Sqrt)
                    act.wait_ge(tail_step, 2 * h + 2)
                    act.activation(t[:, part, :], res[:, 12 + 2 * h:14 + 2 * h, :], ACT.Square).then_inc(tail_squared, 1)

            def root_of(k):
                act.wait_ge(recip_ready, k + 1)
                act.activation(root, corr, ACT.Sqrt).then_inc(root_ready, 1)

            def finish_attention(j):
                if j == 0:
                    act.wait_ge(o_recip, 1)
                    act.activation(o_root, o_corr, ACT.Sqrt).then_inc(o_rooted, 1)
                if j in (5, 6):
                    h = j - 5
                    if h == 0:
                        act.wait_ge(o_turned, 1)
                        act.wait_ge(subln_ready, 1)
                    else:
                        act.wait_ge(o_ready, 1)
                    act.activation(t[:, :, :].rearrange("p b t -> p (b t)"),
                                   ps[:, 4 + 2 * h:6 + 2 * h, :].rearrange("p b t -> p (b t)"), ACT.Copy,
                                   scale=subln).then_inc(o_copied, 1)
                    act.wait_ge(o_copied, h + 1)
                    act.activation(opB[:, 4 * h:4 * h + 4, 0:SEQ], t[:, :, :], ACT.Copy).then_inc(o_hi, 1)
                if j in (8, 13):
                    h = j // 13
                    act.wait_ge(pooled, 4 * h + 4)
                    act.activation(opB[:, 8 + 4 * h:12 + 4 * h, 0:SEQ], z[:, :, :], ACT.Copy).then_inc(pooled_hi, 1)

            def pair(ph, i, r):
                first_pair = ph is PH["qk"] and i == 0
                for j in range(2 * ph.upg):
                    if ph.upg == 1:
                        for half, step in drains_at(ph, j):
                            drain(ph, i, r, half, step)
                    if first_pair and j < 3:
                        xg_part_hi(j + 5)
                    split_hi(ph, i, r, j + LEAD)
                    if ph.kind in ("ab", "pb") and j % 4 == 0:
                        open_gate(ph, i, j // 4)
                    if ph.kind == "slot" and not isinstance(i, int):
                        if j in (1, 5):
                            if j == 5:
                                copy_turned(i, 0)
                            exps(i, j // 5)
                        if j == 8:
                            copy_out(i, 0)
                        if j == 10:
                            copy_turned(i, 1)
                        if j == 13:
                            copy_out(i, 1)
                    if first_pair and j in SQUARES_AT:
                        q = SQUARES_AT.index(j)
                        if q:
                            act.wait_ge(ssq_part, q)
                        if q == 2:
                            act.wait_ge(psum_free, 1)
                        square_res(4 * q)
                    if first_pair and j == 10:
                        act.wait_ge(lam_summed, 1)
                        act.activation(lam_exp, ps[:, 2, 0:2], ACT.Exp).then_inc(lam_exped, 1)
                    if ph.kind == "slot" and isinstance(i, int):
                        finish_attention(j)
                    if has_norm(ph, i) and j == (10 if first_pair else 3):
                        root_of(norm_of[ph.kind])
                    if ph is PH["mix"] and j == 1:
                        drain(ph, i, r, 0, 2)
                    if ph is PH["ab1"] and j == 0:
                        drain(PH["mix"], 0, 0, 1, 2)
                    for half, step in drains_at(ph, j) if ph.upg > 1 else ():
                        drain(ph, i, r, half, step)
                if ph.kind == "ab" and ph.index0 == 2:
                    act.wait_ge(p_loaded, 16)
                    act.activation(p_parts[:, :, 0:SEQ], p_in, ACT.Copy).then_inc(p_hi, 1)

            act.sem_inc(head_done, 1)
            act.dma_start(cols[:, :], d["cols"]).then_inc(cols_loaded, 16)
            act.dma_start(lam_in, d["lam"]).then_inc(lam_loaded, 16)
            for u in range(5):
                xg_part_hi(u)
                split_hi(PH["qk"], 0, 0, u)
            walk(act, pair)
            root_of(3)

        @block.vector
        def _(dve):
            def split_lo(ph, i, r, u):
                n = unit_index(ph, i, r, u)
                if isinstance(n, int) and n >= UNITS:
                    return
                s = slot_of(ph, i, u)
                if isinstance(n, int) and n == 0:
                    for half, hi, lo in ((slice(0, GW), first_hi, first_lo), (slice(GW, UNIT), hi_ready, lo_ready)):
                        dve.wait_ge(hi, 1)
                        dve.tensor_tensor(w_lo[:, 0, half], stage[:, 0, half], w_hi[:, 0, half].bitcast(F32),
                                          ALU.subtract).then_inc(lo, 1)
                    return
                dve.wait_ge(hi_ready, n + 1)
                dve.tensor_tensor(w_lo[:, s, :], stage[:, s, :], w_hi[:, s, :].bitcast(F32),
                                  ALU.subtract).then_inc(lo_ready, 1)

            def lo_part(kind, dst, src, hi, kc):
                dve.wait_ge(z_hi[kind], kc * 2 + 2 if kind == "up" else kc + 1)
                dve.tensor_tensor(dst, src, hi.bitcast(F32), ALU.subtract).then_inc(drained, 1)

            def add_squares(q, k):
                dve.wait_ge(squared, q + (4 * k + 1))
                dve.tensor_reduce(ssq[:, bass.ds(q, 1), :].rearrange("p o t -> p (o t)"),
                                  t[:, :, :].rearrange("p b t -> p t b"), AX.X, ALU.add).then_inc(ssq_part, 1)

            def join_three():
                dve.wait_ge(ssq_part, 15)
                dve.tensor_reduce(sq_sum[:, :], ssq[:, 0:3, :].rearrange("p q t -> p t q"), AX.X, ALU.add).then_inc(three_joined, 1)

            def join_squares(k):
                dve.wait_ge(ssq_part, 4 * (k + 1))
                dve.tensor_reduce(sq_sum[:, :], ssq[:, :, :].rearrange("p q t -> p t q"), AX.X, ALU.add).then_inc(ssq_joined, 1)

            def drain(ph, i, r, half, step):
                kind, g, kc = ph.kind, group_index(ph, i, r, half), kind_index(ph, i, r, half)
                bank = banks(ph, half, i)
                blocks = bass.ds(kc * GB, GB)
                if isinstance(g, int) and g == LAST_GROUP:
                    if step == 1:
                        last_drain(bank)
                    return
                if kind == "v" and step == 0:
                    dve.wait_ge(unit_done, units_summed(ph, i, r, half))
                    into = xv[:, 16 + half * GB:16 + (half + 1) * GB, :].rearrange("p h (t v) -> p t h v", t=2)
                    dve.tensor_tensor(into, ps[:, bank:bank + 2, :].rearrange("p t (h v) -> p t h v", h=GB),
                                      rstd_col.unsqueeze(2).unsqueeze(3).to_broadcast([P, 2, GB, DV]),
                                      ALU.mult).then_inc(psum_free, 1)
                if kind in PAIRED and kind != "wple" and step == 0:
                    dve.wait_ge(unit_done, units_summed(ph, i, r, half))
                    sums4 = ps[:, bank:bank + 2, :].rearrange("p b (n t) -> p (b n) t", n=2)
                    if kind == "mix":
                        dve.wait_ge(drained, ph.drained0)
                        dve.tensor_tensor((z, y)[half][:, :, :], sums4, gains("pool_scale", kc * GB), ALU.mult).then_inc(psum_free, 1)
                    else:
                        into = ug[:, blocks, :] if kind == "slot" else z[:, :, :]
                        dve.tensor_tensor(into, sums4, all_blocks(rstd[:, :]), ALU.mult).then_inc(psum_free, 1)
                if step == 0 and kind not in TWO_BANKS:
                    dve.wait_ge(low_copied, low_count(ph, i, r, half) + 1)
                    dve.tensor_tensor(y[:, :, :], ps[:, bank:bank + GB, 0:SEQ], t[:, :, :], ALU.add).then_inc(psum_free, 1)
                    dve.wait_ge(psum_free, g + 1)
                if step == 1:
                    if kind == "qk":
                        dve.tensor_tensor(xv[:, blocks, :], y[:, :, :], all_blocks(rstd[:, :]), ALU.mult).then_inc(drained, 1)
                    if kind == "ab":
                        dve.wait_ge(sigmoid_ready[kind], kc + 1)
                        dve.tensor_tensor(gate_a[:, blocks, :], gate_a[:, blocks, :], y[:, :, :], ALU.mult).then_inc(drained, 1)
                    if kind == "pb":
                        dve.wait_ge(sigmoid_ready[kind], kc + 1)
                        dve.tensor_tensor(y[:, :, :], y[:, :, :], gate_p[:, blocks, :], ALU.mult).then_inc(stepped[kind], 1)
                        dve.wait_ge(stepped[kind], kc + 1)
                        dve.tensor_tensor(z[:, :, :], y[:, :, :], gate_a[:, blocks, :], ALU.add).then_inc(z_ready[kind], 1)
                    if kind in ("wout", "downl"):
                        if kind == "wout":
                            for q in range(4):
                                dve.wait_ge(x_again[q], 16)
                        dve.tensor_tensor(res[:, blocks, :], res[:, blocks, :], y[:, :, :], ALU.add).then_inc(stepped[kind], 1)
                        dve.wait_ge(stepped[kind], kc + 1)
                        dve.tensor_tensor(z[:, :, :], res[:, blocks, :],
                                          gains("norm_mlp" if kind == "wout" else "norm_ple", kc * GB),
                                          ALU.mult).then_inc(z_ready[kind], 1)
                    if kind == "up":
                        dve.scalar_tensor_tensor(out=z[:, :, :], in0=y[:, :, :], scalar=0.0, in1=all_blocks(rstd[:, :]),
                                                 op0=ALU.max, op1=ALU.mult).then_inc(z_ready[kind], 1)
                    if kind == "down":
                        part = bass.ds(i * 8 + half * GB, GB)
                        dve.tensor_tensor(res[:, part, :], res[:, part, :], y[:, :, :], ALU.add).then_inc(drained, 1)
                    if kind == "ple":
                        dve.wait_ge(sigmoid_ready[kind], kc + 1)
                        dve.tensor_tensor(z[:, :, :], y[:, :, :], gate_a[:, blocks, :], ALU.mult).then_inc(gated, 1)
                        dve.wait_ge(gated, kc + 1)
                        dve.tensor_tensor(res[:, blocks, :], res[:, blocks, :], z[:, :, :], ALU.add).then_inc(stepped[kind], 1)
                if step == 2:
                    if kind in ("wout", "downl", "ple"):
                        norm_no = {"wout": 1, "downl": 2, "ple": 3}[kind]
                        add_squares(kc, norm_no)
                    if kind in ("mix", "wout", "downl"):
                        lo_part(kind, opA[:, blocks, SEQ:], (y if kind == "mix" and half else z)[:, :, :], opA[:, blocks, 0:SEQ], kc)
                    if kind == "pb":
                        lo_part(kind, opB[:, blocks, SEQ:], z[:, :, :], opB[:, blocks, 0:SEQ], kc)
                    if kind == "up":
                        part = bass.ds(i * 8 + half * GB, GB)
                        lo_part(kind, opB[:, part, SEQ:], y[:, :, :], opB[:, part, 0:SEQ], kc)
                    if kind == "ple":
                        dve.tensor_tensor(res[:, blocks, :], res[:, blocks, :], gains("norm_final", kc * GB),
                                          ALU.mult).then_inc(drained, 1)

            def copy_pair(i):
                dve.wait_ge(drained, PH["slot"].drained0)
                dve.wait_ge(psum_free, PH["slot"].group0)
                dve.wait_ge(head_done, i * 6 + 1)
                dve.tensor_copy(qk[:, :, :], xv[:, 0:16, :].rearrange("p (m b) t -> p m b t", b=4)[:, :, bass.ds(i, 1), :]
                                .rearrange("p m o t -> p m (o t)")).then_inc(pair_copied, 1)
                dve.tensor_copy(v_pair[:, :, :], xv[:, bass.ds(i * 2 + 16, 2), :]).then_inc(pair_copied, 1)

            def softmax_in(i, hh):
                h = i * 2 + hh
                dve.wait_ge(scores_ready, h + 1)
                dve.wait_ge(attn_turned, h + 1)
                dve.scalar_tensor_tensor(out=pr[:, :, :], in0=ps[:, 4:6, 0:TRI], scalar=col("score_scale", h),
                                         in1=neg_dist[:, :].unsqueeze(1).to_broadcast([P, 2, TRI]), op0=ALU.mult,
                                         op1=ALU.add).then_inc(scores_biased, 1)
                dve.wait_ge(scores_biased, h + 2)
                dve.tensor_reduce(row_max[:, 0:2], pr[:, :, 0:P], AX.X, ALU.max).then_inc(max_ready, 1)
                dve.tensor_reduce(row_max[:, 2:4], pr[:, :, P:], AX.X, ALU.max).then_inc(max_ready, 1)
                dve.wait_ge(max_ready, h * 2 + 2)
                dve.tensor_scalar(exp_bias, row_max, col("slope", h), -1.0, ALU.mult, ALU.mult).then_inc(bias_ready, 1)

            def softmax_out(i, hh):
                h = i * 2 + hh
                dve.wait_ge(probs_ready, h * 4 + 4)
                dve.reciprocal(recip, sums).then_inc(recip_sums, 1)
                dve.wait_ge(recip_sums, h * 2 + 1)
                dve.wait_ge(neg_lam_ready, 1)
                dve.tensor_scalar(recip_lam, recip.rearrange("p (b m) -> p b m", m=2)[:, :, 1], neg_lam, None,
                                  ALU.mult).then_inc(recip_sums, 1)
                parts = ((0, P), (P, TRI))
                for b, (a, e) in enumerate(parts):
                    dve.tensor_scalar(pr[:, 0, a:e], pr[:, 0, a:e], recip[:, 2 * b:2 * b + 1], None,
                                      ALU.mult).then_inc(first_scaled, 1)
                dve.wait_ge(recip_sums, h * 2 + 2)
                for b, (a, e) in enumerate(parts):
                    dve.wait_ge(first_scaled, h * 2 + (b + 1))
                    dve.scalar_tensor_tensor(out=pr[:, 0, a:e], in0=pr[:, 1, a:e], scalar=recip_lam[:, b:b + 1],
                                             in1=pr[:, 0, a:e], op0=ALU.mult, op1=ALU.add).then_inc(attn_ready, 1)

            def norm(k):
                dve.wait_ge(ssq_summed, k + 1)
                bank = norm_bank(k)
                dve.tensor_scalar(ms, ps[:, bank, 0:2], 1.0 / D, EPS, ALU.mult, ALU.add).then_inc(ms_ready, 1)
                dve.wait_ge(ms_ready, k + 1)
                dve.reciprocal(corr, ms).then_inc(recip_ready, 1)
                dve.wait_ge(root_ready, k + 1)
                n = 3 * k
                dve.tensor_tensor(corr, root, root, ALU.mult).then_inc(newton, 1)
                dve.wait_ge(newton, n + 1)
                dve.scalar_tensor_tensor(out=corr, in0=corr, scalar=-0.5, in1=ms, op0=ALU.mult, op1=ALU.mult).then_inc(newton, 1)
                dve.wait_ge(newton, n + 2)
                dve.scalar_tensor_tensor(out=rstd_col, in0=corr, scalar=1.5, in1=root, op0=ALU.add, op1=ALU.mult).then_inc(newton, 1)
                dve.wait_ge(newton, n + 3)
                for h in range(2):
                    dve.tensor_scalar(diag[:, h * P:(h + 1) * P], ident[:, :], rstd_col[:, h:h + 1], None,
                                      ALU.mult).then_inc(diag_ready, 1)

            def keep_rstd(k):
                dve.wait_ge(rstd_spread, k + 1)
                dve.tensor_copy(rstd[:, :], ps[:, norm_bank(k), 0:SEQ]).then_inc(rstd_ready, 1)
                dve.wait_ge(rstd_ready, k + 1)

            def last_drain(bank):
                for h in range(2):
                    dve.wait_ge(unit_done if h else front_summed, UNITS - 1 if h else 1)
                    dve.tensor_tensor(z[:, 2 * h:2 * h + 2, :], ps[:, bank + h, :].rearrange("p (n t) -> p n t", n=2),
                                      rstd[:, :].unsqueeze(1).to_broadcast([P, 2, SEQ]), ALU.mult).then_inc(tail_scaled, 1)
                    dve.wait_ge(tail_gate, h + 1)
                    dve.tensor_tensor(z[:, 2 * h:2 * h + 2, :], y[:, 2 * h:2 * h + 2, :],
                                      gate_a[:, 12 + 2 * h:14 + 2 * h, :], ALU.mult).then_inc(tail_step, 1)
                    dve.wait_ge(tail_step, 2 * h + 1)
                    dve.tensor_tensor(res[:, 12 + 2 * h:14 + 2 * h, :], res[:, 12 + 2 * h:14 + 2 * h, :],
                                      z[:, 2 * h:2 * h + 2, :], ALU.add).then_inc(tail_step, 1)

            def finish_attention(j):
                if j == 0:
                    dve.wait_ge(head_done, 3 * HEADS + 1)
                    dve.tensor_scalar(o_ms, o_ssq, 1.0 / DV, EPS, ALU.mult, ALU.add).then_inc(o_ms_ready, 1)
                    dve.wait_ge(o_ms_ready, 1)
                    dve.reciprocal(o_corr, o_ms).then_inc(o_recip, 1)
                if j == 1:
                    dve.wait_ge(o_rooted, 1)
                    dve.tensor_tensor(o_corr, o_root, o_root, ALU.mult).then_inc(o_newton, 1)
                    dve.wait_ge(o_newton, 1)
                    dve.tensor_tensor(o_corr, o_corr, o_ms, ALU.mult).then_inc(o_newton, 1)
                    dve.wait_ge(o_newton, 2)
                    dve.tensor_scalar(o_corr, o_corr, -0.5, 1.5, ALU.mult, ALU.add).then_inc(o_newton, 1)
                    dve.wait_ge(o_newton, 3)
                    dve.tensor_tensor(o_ssq, o_root, o_corr, ALU.mult).then_inc(o_newton, 1)
                if j == 2:
                    dve.wait_ge(o_newton, 4)
                    o = xv[:, 16:24, :].rearrange("p h (b v) -> p (h b) v", b=2)
                    dve.tensor_tensor(o, o, o_ssq.unsqueeze(2).to_broadcast([P, 16, DV]), ALU.mult).then_inc(o_scaled, 1)
                if j in (5, 6):
                    h = j - 5
                    dve.wait_ge(o_hi, h + 1)
                    dve.tensor_tensor(opB[:, 4 * h:4 * h + 4, SEQ:], t[:, :, :], opB[:, 4 * h:4 * h + 4, 0:SEQ].bitcast(F32),
                                      ALU.subtract).then_inc(o_ready, 1)
                if j in (3, 7, 9, 11):
                    pool_group((3, 7, 9, 11).index(j))
                if j in (8, 13):
                    h = j // 13
                    dve.wait_ge(pooled_hi, h + 1)
                    dve.tensor_tensor(opB[:, 8 + 4 * h:12 + 4 * h, SEQ:], z[:, :, :],
                                      opB[:, 8 + 4 * h:12 + 4 * h, 0:SEQ].bitcast(F32), ALU.subtract).then_inc(pooled_ready, 1)

            def x_buf(e):
                return z[:, 2 * (e % 2):2 * (e % 2) + 2, :]

            def scale_x(e):
                dve.wait_ge(x_loaded[e], 16)
                dve.tensor_tensor(x_buf(e), res[:, 2 * e:2 * e + 2, :], gains("norm_mix", 2 * e, 2), ALU.mult).then_inc(xg_scaled, 1)

            def xg_part_lo(e):
                x_lo(e)
                if e < 7:
                    dve.wait_ge(xg_ready, e)
                    scale_x(e + 1)

            def x_lo(e):
                dve.wait_ge(xg_hi, e + 1)
                dve.tensor_tensor(opA[:, 2 * e:2 * e + 2, SEQ:], x_buf(e), opA[:, 2 * e:2 * e + 2, 0:SEQ].bitcast(F32),
                                  ALU.subtract).then_inc(xg_ready, 1)

            def lam_product():
                dve.wait_ge(lam_loaded, 16)
                dve.tensor_tensor(lam_prod, lam_in[:, 0:2], lam_in[:, 2:4], ALU.mult).then_inc(lam_step, 1)
                dve.tensor_scalar(subln, col("subln"), 1.0 - LAM_INIT, None, ALU.mult).then_inc(subln_ready, 1)

            def lam_value():
                dve.wait_ge(lam_exped, 1)
                dve.scalar_tensor_tensor(out=neg_lam, in0=lam_exp[:, 1:2], scalar=-LAM_INIT, in1=lam_exp[:, 0:1],
                                         op0=ALU.add, op1=ALU.subtract).then_inc(neg_lam_ready, 1)

            def pool_group(g):
                w = WINDOWS[g]
                if g == 2:
                    dve.wait_ge(pooled_ready, 1)
                dve.wait_ge(psum_free, PH["slot"].group0 + 2)
                u = ug[:, 2 * g:2 * g + 2, :]
                cur, reach, n = u, 1, 0
                steps = sum(2 * (v.bit_length() - 1) + 1 for v in WINDOWS[:g])
                while reach < w:
                    nxt = y[:, 2 * (n % 2):2 * (n % 2) + 2, :]
                    dve.tensor_tensor(nxt[:, :, reach:], cur[:, :, reach:], cur[:, :, 0:SEQ - reach], ALU.add).then_inc(pool_step, 1)
                    dve.tensor_copy(nxt[:, :, 0:reach], cur[:, :, 0:reach]).then_inc(pool_step, 1)
                    steps += 2
                    dve.wait_ge(pool_step, steps)
                    cur, reach, n = nxt, 2 * reach, n + 1
                o = z[:, 2 * (g % 2):2 * (g % 2) + 2, :]
                head = 16
                inv = cols[:, COLS["inv_count"][0] + g * head:COLS["inv_count"][0] + (g + 1) * head]
                dve.scalar_tensor_tensor(out=o[:, :, head:], in0=cur[:, :, head:], scalar=1.0 / w, in1=u[:, :, head:],
                                         op0=ALU.mult, op1=ALU.subtract).then_inc(pooled, 1)
                dve.tensor_tensor(o[:, :, 0:head], cur[:, :, 0:head], inv.unsqueeze(1).to_broadcast([P, 2, head]),
                                  ALU.mult).then_inc(pool_step, 1)
                dve.wait_ge(pool_step, steps + 1)
                dve.tensor_tensor(o[:, :, 0:head], o[:, :, 0:head], u[:, :, 0:head], ALU.subtract).then_inc(pooled, 1)

            def pair(ph, i, r):
                first_pair = ph is PH["qk"] and i == 0
                for j in range(2 * ph.upg):
                    if ph.upg == 1:
                        for half, step in drains_at(ph, j):
                            drain(ph, i, r, half, step)
                    if first_pair and j < 3:
                        xg_part_lo(j + 5)
                    if ph.kind == "slot" and not isinstance(i, int) and j == 0:
                        copy_pair(i)
                    split_lo(ph, i, r, j + LEAD)
                    if ph.kind == "slot" and not isinstance(i, int):
                        if j in (1, 5):
                            softmax_in(i, j // 5)
                        if j in (2, 6):
                            softmax_out(i, j // 6)
                    if ph.kind == "slot" and isinstance(i, int):
                        finish_attention(j)
                    if ph is PH["ple"] and i == 1 and j == 12:
                        join_three()
                    if first_pair:
                        if j == 2:
                            lam_product()
                        if j in SQUARES_AT:
                            add_squares(SQUARES_AT.index(j), 0)
                        if j == 8:
                            join_squares(0)
                        if j == 10:
                            norm(0)
                            lam_value()
                        if j == 12:
                            keep_rstd(0)
                            drain(ph, i, r, 0, 1)
                    elif has_norm(ph, i):
                        if j == 1:
                            join_squares(norm_of[ph.kind])
                        if j == 3:
                            norm(norm_of[ph.kind])
                        if j == 5:
                            keep_rstd(norm_of[ph.kind])
                    if ph is PH["mix"] and j == 1:
                        drain(ph, i, r, 0, 2)
                    if ph is PH["ab1"] and j == 0:
                        drain(PH["mix"], 0, 0, 1, 2)
                    for half, step in drains_at(ph, j) if ph.upg > 1 else ():
                        if not (first_pair and half == 0 and step == 1):
                            drain(ph, i, r, half, step)
                if ph.kind == "ab" and ph.index0 == 2:
                    dve.wait_ge(p_hi, 1)
                    dve.tensor_tensor(p_parts[:, :, SEQ:], p_in, p_parts[:, :, 0:SEQ].bitcast(F32),
                                      ALU.subtract).then_inc(p_ready, 1)

            dve.sem_inc(scores_biased, 1)
            dve.wait_ge(cols_loaded, 16)
            scale_x(0)
            for u in range(5):
                if u:
                    xg_part_lo(u)
                else:
                    x_lo(0)
                split_lo(PH["qk"], 0, 0, u)
                if u == 0:
                    scale_x(1)
            walk(dve, pair)
            norm(3)
            dve.wait_ge(rstd_spread, 4)
            spread_rstd = ps[:, norm_bank(3), 0:SEQ]
            for b0, n in FINAL_PIECES:
                dve.tensor_tensor(res[:, b0:b0 + n, :], res[:, b0:b0 + n, :],
                                  spread_rstd.unsqueeze(1).to_broadcast([P, n, SEQ]), ALU.mult).then_inc(final_scaled, 1)
            for b in range(DB - GB, DB):
                dve.scalar_tensor_tensor(out=res[:, b, :], in0=res[:, b, :], scalar=col("norm_final", b), in1=spread_rstd,
                                         op0=ALU.mult, op1=ALU.mult).then_inc(final_scaled, 1)


def kernel(**inputs):
    import numpy as np
    import concourse.bacc as bacc
    from concourse.bass_utils import run_bass_kernel_spmd

    a = {k: np.asarray(v) for k, v in inputs.items()}

    def by_block(v):
        return v.reshape(-1, P).T

    heads = np.arange(HEADS)
    slope = (2.0 ** (-8.0 * (heads + 1) / HEADS)).astype(np.float32)
    counts = np.stack([np.minimum(np.arange(16) + 1, w) for w in WINDOWS]).astype(np.float32)
    shapes_only = np.concatenate([DQK ** -0.5 / slope, slope, (1.0 / counts).ravel()]).astype(np.float32)
    arrays = {
        "x": np.ascontiguousarray(a["x"][0].T),
        "p": np.ascontiguousarray(a["p"][0, 0].T),
        "cols": np.ascontiguousarray(np.concatenate(
            [by_block(a["norm_mix_g"][0]), by_block(a["norm_mlp_g"][0]), by_block(a["norm_ple_g"][0]),
             by_block(a["final_norm_g"]), by_block(a["pool_scale"][0]), by_block(a["subln_g"][0]),
             np.broadcast_to(shapes_only, (P, shapes_only.size))], axis=1)),
        "lam": np.ascontiguousarray(np.stack(
            [a["lambda_q1"][0], a["lambda_q2"][0], a["lambda_k1"][0], a["lambda_k2"][0]], axis=1)),
        "pool_grp_w": a["pool_grp_w"].reshape(-1, 256),
    }
    for name in ("w_in", "w_attn_br", "w_pool_br", "w_out", "w_mlp_up", "w_mlp_down", "w_ple", "w_ple_gate"):
        arrays[name] = a[name][0]
    nc = bacc.Bacc("TRN2", target_bir_lowering=False, num_devices=1)
    aps = {name: nc.dram_tensor(f"in_{name}", v.shape, F32, kind="ExternalInput").ap() for name, v in arrays.items()}
    out = nc.dram_tensor("out", (D, SEQ), F32, kind="ExternalOutput").ap()
    build(nc, aps, out)
    got = run_bass_kernel_spmd(nc, [{f"in_{name}": v for name, v in arrays.items()}], core_ids=[0])
    return np.ascontiguousarray(got.results[0]["out"].T)[None]
```
